# Optimizing a Trainium2 kernel written in Bass

```python
import math
import jax, jax.numpy as jnp
from jax import lax
import numpy as np

D_MODEL = 1024
BATCH = 1
SEQ = 256
DEPTH = 2

HEAD_DIM = 64
CHUNK = 64
Q_BLOCK = 128
N_HEADS_A = 8
N_HEADS_B = 8
N_HEADS_C = 8
N_HEADS_D = 8
N_KV_D = 2
LEFT_CHUNKS_C = 8
REL_CLIP = 128
WINDOW_D = 128
WINDOW_CHUNKS_D = WINDOW_D // CHUNK
D_FF = 2816
D_PLE = 256
EPS = 1e-6
NEG = -1e30

A_W = N_HEADS_A * HEAD_DIM
B_W = N_HEADS_B * HEAD_DIM
C_W = N_HEADS_C * HEAD_DIM
D_W = N_HEADS_D * HEAD_DIM
KV_W = N_KV_D * HEAD_DIM
MIX_EVEN = A_W + B_W
MIX_ODD = C_W + D_W
IN_EVEN = 3 * A_W + N_HEADS_A + 3 * B_W
IN_ODD = 3 * C_W + D_W + 2 * KV_W

kernel_name = 'hybrid_streaming_fox_sb_chunk_swa'

def rmsnorm(x, g):
    xf = x.astype(jnp.float32)
    y = xf * lax.rsqrt(jnp.mean(xf * xf, axis=-1, keepdims=True) + EPS)
    return (y * g.astype(jnp.float32)).astype(x.dtype)

def swiglu(x, w_gu, w_down):
    g, u = jnp.split(x @ w_gu, 2, axis=-1)
    return (jax.nn.silu(g) * u) @ w_down

def split_cols(t, sizes):
    return jnp.split(t, [int(c) for c in np.cumsum(sizes)[:-1]], axis=-1)

def heads(t, n):
    b, s, _ = t.shape
    return t.reshape(b, s, n, HEAD_DIM).transpose(0, 2, 1, 3)

def unheads(t):
    b, n, s, hd = t.shape
    return t.transpose(0, 2, 1, 3).reshape(b, s, n * hd)

def forgetting_attention(q, k, v, f_logit, b_f):
    b, h, s, hd = q.shape
    nb = s // Q_BLOCK
    log_f = jax.nn.log_sigmoid(f_logit.astype(jnp.float32) + b_f.astype(jnp.float32))
    F = jnp.cumsum(log_f, axis=1).transpose(0, 2, 1)
    qb = q.reshape(b, h, nb, Q_BLOCK, hd).transpose(2, 0, 1, 3, 4)
    Fq = F.reshape(b, h, nb, Q_BLOCK).transpose(2, 0, 1, 3)
    kpos = jnp.arange(s)
    scale = HEAD_DIM ** -0.5

    def block(args):
        qi, Fi, bi = args
        qpos = bi * Q_BLOCK + jnp.arange(Q_BLOCK)
        logits = (jnp.einsum('bhqd,bhkd->bhqk', qi, k).astype(jnp.float32) * scale
                  + Fi[..., None] - F[:, :, None, :])
        logits = jnp.where(kpos[None, :] <= qpos[:, None], logits, NEG)
        w = jax.nn.softmax(logits, axis=-1)
        return jnp.einsum('bhqk,bhkd->bhqd', w.astype(v.dtype), v)

    out = lax.map(block, (qb, Fq, jnp.arange(nb)))
    return out.transpose(1, 2, 0, 3, 4).reshape(b, h, s, hd)

def stick_breaking_attention(q, k, v):
    b, h, s, hd = q.shape
    nb = s // Q_BLOCK
    qb = q.reshape(b, h, nb, Q_BLOCK, hd).transpose(2, 0, 1, 3, 4)
    kpos = jnp.arange(s)
    scale = HEAD_DIM ** -0.5

    def block(args):
        qi, bi = args
        qpos = bi * Q_BLOCK + jnp.arange(Q_BLOCK)
        z = jnp.einsum('bhqd,bhkd->bhqk', qi, k).astype(jnp.float32) * scale
        strict = kpos[None, :] < qpos[:, None]
        log_1m = jnp.where(strict, jax.nn.log_sigmoid(-z), 0.0)
        incl = lax.cumsum(log_1m, axis=3, reverse=True)
        excl = jnp.concatenate([incl[..., 1:], jnp.zeros_like(incl[..., :1])], axis=-1)
        a = jnp.where(strict, jnp.exp(jax.nn.log_sigmoid(z) + excl), 0.0)
        return jnp.einsum('bhqk,bhkd->bhqd', a.astype(v.dtype), v)

    out = lax.map(block, (qb, jnp.arange(nb)))
    return out.transpose(1, 2, 0, 3, 4).reshape(b, h, s, hd)

def chunk_band(t, n_left):
    b, h, s, hd = t.shape
    nc = s // CHUNK
    tp = jnp.pad(t.reshape(b, h, nc, CHUNK, hd), ((0, 0), (0, 0), (n_left, 0), (0, 0), (0, 0)))
    band = jnp.stack([tp[:, :, o:o + nc] for o in range(n_left + 1)], axis=3)
    return band.reshape(b, h, nc, (n_left + 1) * CHUNK, hd)

def band_geometry(nc, n_left):
    band = (n_left + 1) * CHUNK
    m = jnp.arange(band)
    rel = n_left * CHUNK + jnp.arange(CHUNK)[:, None] - m[None, :]
    valid = ((jnp.arange(nc)[:, None] - n_left) * CHUNK + m[None, :]) >= 0
    return rel, valid

def chunked_relbias_attention(q, k, v, rel_table):
    b, h, s, hd = q.shape
    nc = s // CHUNK
    qc = q.reshape(b, h, nc, CHUNK, hd)
    kb = chunk_band(k, LEFT_CHUNKS_C)
    vb = chunk_band(v, LEFT_CHUNKS_C)
    rel, valid = band_geometry(nc, LEFT_CHUNKS_C)
    bias = rel_table.astype(jnp.float32)[:, jnp.clip(rel, -REL_CLIP, REL_CLIP) + REL_CLIP]
    logits = (jnp.einsum('bhcqd,bhckd->bhcqk', qc, kb).astype(jnp.float32) * HEAD_DIM ** -0.5
              + bias[:, None])
    logits = jnp.where(valid[:, None, :], logits, NEG)
    w = jax.nn.softmax(logits, axis=-1)
    return jnp.einsum('bhcqk,bhckd->bhcqd', w.astype(v.dtype), vb).reshape(b, h, s, hd)

def sliding_window_gqa(q, k, v, sink):
    b, hq, s, hd = q.shape
    hkv = k.shape[1]
    g = hq // hkv
    nc = s // CHUNK
    qc = q.reshape(b, hkv, g, nc, CHUNK, hd)
    kb = chunk_band(k, WINDOW_CHUNKS_D - 1)
    vb = chunk_band(v, WINDOW_CHUNKS_D - 1)
    rel, valid = band_geometry(nc, WINDOW_CHUNKS_D - 1)
    slopes = jnp.exp2(-8.0 * jnp.arange(1, hq + 1, dtype=jnp.float32) / hq)
    alibi = (-slopes[:, None, None] * jnp.abs(rel).astype(jnp.float32)).reshape(hkv, g, 1, CHUNK, -1)
    logits = (jnp.einsum('bkgcqd,bkcmd->bkgcqm', qc, kb).astype(jnp.float32) * HEAD_DIM ** -0.5
              + alibi)
    logits = jnp.where(valid[:, None, :], logits, NEG)
    sink_l = jnp.broadcast_to(sink.astype(jnp.float32).reshape(hkv, g, 1, 1, 1), logits.shape[:-1] + (1,))
    w = jax.nn.softmax(jnp.concatenate([logits, sink_l], axis=-1), axis=-1)[..., :-1]
    return jnp.einsum('bkgcqm,bkcmd->bkgcqd', w.astype(v.dtype), vb).reshape(b, hq, s, hd)

def even_mixer(h, w_in, b_f, w_out):
    qa, ka, va, fa, qb, kb, vb = split_cols(h @ w_in, [A_W, A_W, A_W, N_HEADS_A, B_W, B_W, B_W])
    oa = forgetting_attention(heads(qa, N_HEADS_A), heads(ka, N_HEADS_A), heads(va, N_HEADS_A), fa, b_f)
    ob = stick_breaking_attention(heads(qb, N_HEADS_B), heads(kb, N_HEADS_B), heads(vb, N_HEADS_B))
    return jnp.concatenate([unheads(oa), unheads(ob)], axis=-1) @ w_out

def odd_mixer(h, w_in, rel_table, sink, w_out):
    qc, kc, vc, qd, kd, vd = split_cols(h @ w_in, [C_W, C_W, C_W, D_W, KV_W, KV_W])
    oc = chunked_relbias_attention(heads(qc, N_HEADS_C), heads(kc, N_HEADS_C), heads(vc, N_HEADS_C), rel_table)
    od = sliding_window_gqa(heads(qd, N_HEADS_D), heads(kd, N_KV_D), heads(vd, N_KV_D), sink)
    return jnp.concatenate([unheads(oc), unheads(od)], axis=-1) @ w_out

def setup_inputs(seed: int = 0) -> dict:
    key = jax.random.key(seed)
    ks = jax.random.split(key, 24)
    f32 = jnp.float32
    ne = (DEPTH + 1) // 2
    no = DEPTH // 2

    def w(k, shape, fan_in):
        return jax.random.normal(k, shape, f32) * fan_in ** -0.5

    def gain(k, shape):
        return 1.0 + 0.01 * jax.random.normal(k, shape, f32)

    return {
        'x': jax.random.normal(ks[0], (BATCH, SEQ, D_MODEL), f32),
        'p': jax.random.normal(ks[1], (DEPTH, BATCH, SEQ, D_PLE), f32),
        'ln_ffn1': gain(ks[2], (DEPTH, D_MODEL)),
        'w_ffn1_gu': w(ks[3], (DEPTH, D_MODEL, 2 * D_FF), D_MODEL),
        'w_ffn1_down': w(ks[4], (DEPTH, D_FF, D_MODEL), D_FF),
        'ln_mix': gain(ks[5], (DEPTH, D_MODEL)),
        'w_in_even': w(ks[6], (ne, D_MODEL, IN_EVEN), D_MODEL),
        'b_forget': 1.0 + 5.0 * jax.random.uniform(ks[7], (ne, N_HEADS_A), f32),
        'w_out_even': w(ks[8], (ne, MIX_EVEN, D_MODEL), MIX_EVEN),
        'w_in_odd': w(ks[9], (no, D_MODEL, IN_ODD), D_MODEL),
        'rel_bias': 0.1 * jax.random.normal(ks[10], (no, N_HEADS_C, 2 * REL_CLIP + 1), f32),
        'sinks': 0.5 * jax.random.normal(ks[11], (no, N_HEADS_D), f32),
        'w_out_odd': w(ks[12], (no, MIX_ODD, D_MODEL), MIX_ODD),
        'ln_ffn2': gain(ks[13], (DEPTH, D_MODEL)),
        'w_ffn2_gu': w(ks[14], (DEPTH, D_MODEL, 2 * D_FF), D_MODEL),
        'w_ffn2_down': w(ks[15], (DEPTH, D_FF, D_MODEL), D_FF),
        'ln_ple': gain(ks[16], (DEPTH, D_MODEL)),
        'w_ple_gate': w(ks[17], (DEPTH, D_MODEL, D_MODEL), D_MODEL),
        'w_ple_proj': w(ks[18], (DEPTH, D_PLE, D_MODEL), D_PLE),
        'ln_final': gain(ks[19], (D_MODEL,)),
    }

def reference(x, p, ln_ffn1, w_ffn1_gu, w_ffn1_down, ln_mix, w_in_even, b_forget, w_out_even,
              w_in_odd, rel_bias, sinks, w_out_odd, ln_ffn2, w_ffn2_gu, w_ffn2_down,
              ln_ple, w_ple_gate, w_ple_proj, ln_final):
    for i in range(DEPTH):
        j = i // 2
        x = x + 0.5 * swiglu(rmsnorm(x, ln_ffn1[i]), w_ffn1_gu[i], w_ffn1_down[i])
        h = rmsnorm(x, ln_mix[i])
        if i % 2 == 0:
            x = x + even_mixer(h, w_in_even[j], b_forget[j], w_out_even[j])
        else:
            x = x + odd_mixer(h, w_in_odd[j], rel_bias[j], sinks[j], w_out_odd[j])
        x = x + 0.5 * swiglu(rmsnorm(x, ln_ffn2[i]), w_ffn2_gu[i], w_ffn2_down[i])
        gate = jax.nn.sigmoid(rmsnorm(x, ln_ple[i]) @ w_ple_gate[i])
        x = x + gate * (p[i] @ w_ple_proj[i])
    return rmsnorm(x, ln_final)


_drawn_inputs = setup_inputs


def setup_inputs(seed=0):
    import zlib

    import numpy as np

    out = dict(_drawn_inputs(seed))
    spreads = {}
    factors = {'ln_ffn1': 8.0,
     'ln_mix': 8.0,
     'rel_bias': 31.774,
     'sinks': 7.806,
     'ln_ffn2': 8.0,
     'ln_ple': 64.0,
     'ln_final': 32.215}
    for name, (base, spread) in spreads.items():
        noise = np.random.default_rng([zlib.crc32(name.encode()), seed]).standard_normal(out[name].shape)
        drawn = base * np.exp(spread * noise) if base else spread * noise
        out[name] = __import__('jax').numpy.asarray(drawn.astype(out[name].dtype))
    for name, factor in factors.items():
        out[name] = (out[name] * factor).astype(out[name].dtype)
    return out
```

```python
from contextlib import ExitStack

import concourse.bass as bass
from concourse import mybir

ALU = mybir.AluOpType
ACT = mybir.ActivationFunctionType
AX_X = mybir.AxisListType.X
F32 = mybir.dt.float32
F32R = mybir.dt.float32r
BF16 = mybir.dt.bfloat16
I32 = mybir.dt.int32

P = 128
D_MODEL, SEQ, D_FF, D_PLE, DEPTH = 1024, 256, 2816, 256, 2
HD = 64
HEADS = 8
GROUP_W = HEADS * HD
CHUNK = 64
REL_CLIP = 128
KD = D_MODEL // P
KF = D_FF // P
KPLE = D_PLE // P
TOK = SEQ // P
EPS = 1e-6
BIG = 1e30
RING = 4
CH = KD * 256
CH_DOWN = (KF // 2) * P
LOGITS = 3 * P
MAGIC = 0x5F3759DF
NO_SIGN = 0x7FFFFFFF
SCALE = HD ** -0.5


class Phase:

    def __init__(self, kind, layer, which, c0, chunks, units):
        self.kind, self.layer, self.which, self.c0, self.chunks = kind, layer, which, c0, chunks
        self.unit = units


def plan():
    phases, c = [], 0
    for layer in range(DEPTH):
        for kind, which, chunks, unit in (
            ("gu", 0, 2 * KF // 2, CH // 2), ("down", 0, 2 * KD, CH_DOWN // 2),
            ("in", 0, 12 if layer == 0 else 9, CH // 2), ("out", 0, 4, CH // 2),
            ("gu", 1, 2 * KF // 2, CH // 2), ("down", 1, 2 * KD, CH_DOWN // 2),
            ("proj", 0, 1, CH // 2), ("gate", 0, 4, CH // 2),
        ):
            phases.append(Phase(kind, layer, which, c, chunks, unit))
            c += chunks
    return phases, c


def in_tiles(layer):
    tiles = []
    chunk = 0
    for group in range(2):
        neg = not (layer == 0 and group == 1)
        scale = -SCALE if neg else SCALE
        if layer == 1 and group == 1:
            tiles.append((chunk, 0, "k", 4, 1.0))
            for t in range(TOK):
                tiles.append((chunk, P, "vd", t, 1.0))
            chunk += 1
            for j in range(2):
                for n in range(2):
                    tiles.append((chunk, n * P, "q", 4 + 2 * j + n, scale))
                chunk += 1
            break
        for what in "qkv":
            for j in range(2):
                for n in range(2):
                    if what == "v":
                        tiles.append((chunk, 0, "v", (group, j, n), 1.0))
                    else:
                        tiles.append((chunk, n * P, what, 4 * group + 2 * j + n, scale if what == "q" else 1.0))
                chunk += 1
    return tiles


PLE_TILES = [("p", m) for m in range(KD)] + [("g", m) for m in range(KD)]


def ple_bank(kind, m):
    return m % 4 if kind == "g" else (m + 4) % 6


def chunk_ends(phases):
    ends, T = [], KD
    for ph in phases:
        if ph.kind == "down":
            ends += [T + r // 2 + 1 for r in range(ph.chunks)]
            T += KD
        elif ph.kind == "in":
            tiles = in_tiles(ph.layer)
            ends += [T + sum(t[0] <= r for t in tiles) for r in range(ph.chunks)]
            T += len(tiles)
        elif ph.kind == "out":
            ends += [T + KD + 2 * r + 2 for r in range(ph.chunks)]
            T += 2 * KD
        elif ph.kind == "proj":
            ends.append(T + PLE_TILES.index(("p", KD - 1)) + 1)
        elif ph.kind == "gate":
            ends += [T + PLE_TILES.index(("g", 2 * r + 1)) + 1 for r in range(ph.chunks)]
            T += len(PLE_TILES)
        else:
            ends += [T + 2 * r + 2 for r in range(ph.chunks)]
            T += 2 * ph.chunks
    return ends


def trunk(nc, x, p, ln_ffn1, w_ffn1_gu, w_ffn1_down, ln_mix, w_in_even, b_forget, w_out_even, w_in_odd,
          rel_bias, sinks, w_out_odd, ln_ffn2, w_ffn2_gu, w_ffn2_down, ln_ple, w_ple_gate, w_ple_proj,
          ln_final, out):
    phases, n_chunks = plan()
    n_ffn = 0
    for ph in phases:
        if ph.kind == "gu":
            ph.F0 = KF * n_ffn
            n_ffn += 1
        elif ph.kind == "down":
            ph.F0 = KF * (n_ffn - 1)
    tile_end = chunk_ends(phases)

    rel_scratch = nc.dram_tensor("rel_scratch", [HEADS, 3 * P], F32)

    with ExitStack() as ctx:
        def sb(name, shape, dt):
            return ctx.enter_context(nc.sbuf_tensor(name, shape, dt))

        def sem(name):
            return ctx.enter_context(nc.semaphore(name))

        xT = sb("xT", [P, KD, SEQ], F32)
        xsA = sb("xsA", [P, KD, 2, SEQ], F32R)
        raw = sb("raw", [P, RING, CH], F32)
        wsp = sb("wsp", [P, RING, 2, CH], F32R)

        with ExitStack() as region:
            osp = region.enter_context(nc.sbuf_tensor("osp", [P, KD, 2, SEQ], F32R))
            qT = region.enter_context(nc.sbuf_tensor("qT", [P, 8, SEQ], F32))
            kT = region.enter_context(nc.sbuf_tensor("kT", [P, 8, SEQ], F32))
            vN = region.enter_context(nc.sbuf_tensor("vN", [P, TOK, 2 * GROUP_W], F32))
        with ExitStack() as region:
            hankel = region.enter_context(nc.sbuf_tensor("hankel", [P, HEADS, 257], F32))
        with ExitStack() as region:
            xin = region.enter_context(nc.sbuf_tensor("xin", [P, TOK, D_MODEL], F32))
            gin = region.enter_context(nc.sbuf_tensor("gin", [P, P], F32))
            proj = region.enter_context(nc.sbuf_tensor("proj", [P, KD, SEQ], F32))
            yT = region.enter_context(nc.sbuf_tensor("yT", [P, KD, SEQ], F32))
            yN = region.enter_context(nc.sbuf_tensor("yN", [P, TOK, D_MODEL], F32))
            rel_sb = region.enter_context(nc.sbuf_tensor("rel_sb", [HEADS, 3 * P], F32))
        hff = sb("hff", [P, KF, 2, SEQ], F32R)

        with ExitStack() as region:
            xsB = region.enter_context(nc.sbuf_tensor("xsB", [P, KD, 2, SEQ], F32R))
        with ExitStack() as region:
            pin = region.enter_context(nc.sbuf_tensor("pin", [P, TOK, D_PLE], F32))
            region.enter_context(nc.sbuf_tensor("pin_pad", [P, 6 * 2 * SEQ - TOK * D_PLE], F32))
            psp = region.enter_context(nc.sbuf_tensor("psp", [P, KPLE, 2, SEQ], F32R))
        bias = sb("bias", [P, HEADS, LOGITS], F32)
        probs = sb("probs", [P, 2, LOGITS], F32)
        probsT = sb("probsT", [P, 2, LOGITS], F32)

        bias_swa = sb("bias_swa", [P, 2, LOGITS], F32)
        mask_causal = sb("mask_causal", [P, LOGITS], F32)
        mask_chunk = sb("mask_chunk", [P, LOGITS], F32)
        dist_swa = sb("dist_swa", [P, LOGITS], F32)
        mask_sb = sb("mask_sb", [P, P], BF16)
        identb = sb("identb", [P, P], BF16)
        ident = sb("ident", [P, P], F32)
        cumtri = sb("cumtri", [P, 2 * P], F32)
        negtri = sb("negtri", [P, P], F32)
        negones = sb("negones", [P, P], F32)
        gains = sb("gains", [P, (4 * DEPTH + 1) * KD], F32)
        gate_n = sb("gate_n", [P, 2, SEQ], F32)
        silu = sb("silu", [P, SEQ], F32)
        hidden = sb("hidden", [P, SEQ], F32)
        tile_s = sb("tile_s", [P, SEQ], F32)
        sq = sb("sq", [P, 2, SEQ], F32)
        sqsum = sb("sqsum", [P, SEQ], F32)
        rstd = sb("rstd", [P, SEQ], F32)
        rdiag = sb("rdiag", [P, TOK, P], F32)
        var = sb("var", [P, 2], F32)
        nhalf = sb("nhalf", [P, 2], F32)
        rcol = sb("rcol", [P, 2], F32)
        rtmp = sb("rtmp", [P, 2], F32)
        wf_raw = sb("wf_raw", [P, KD, HEADS], F32)
        wf = sb("wf", [P, 2, KD, HEADS], F32R)
        bf = sb("bf", [P, HEADS], F32)
        nsink = sb("nsink", [P, HEADS], F32)
        fl = sb("fl", [P, TOK, HEADS], F32)
        fa = sb("fa", [P, TOK, HEADS], F32)
        logf = sb("logf", [P, TOK, HEADS], F32)
        fcum = sb("fcum", [P, TOK, HEADS], F32)
        negmax = sb("negmax", [P, 2, 2], F32)
        rowsum = sb("rowsum", [P, 4, 2], F32)
        sinkexp = sb("sinkexp", [P, 4, 2], F32)
        rinv = sb("rinv", [P, 4, 2], F32)

        ps = ctx.enter_context(nc.psum_tensor("ps", [P, 8, 512], F32))
        BANK_S, BANK_PT, BANK_F = 4, 6, 7
        BANK_O = (3, 7)
        BANK_COL, BANK_ROW = 7, 6

        landed = [sem(f"landed{s}") for s in range(RING)]
        hi = sem("hi")
        lo = sem("lo")
        tile_done = sem("tile_done")
        in_x, in_g, in_p, in_small = sem("in_x"), sem("in_g"), sem("in_p"), sem("in_small")
        in_rel, rel_out, rel_back, rel_ext = sem("in_rel"), sem("rel_out"), sem("rel_back"), sem("rel_ext")
        consts = sem("consts")
        dist_abs, dist_done = sem("dist_abs"), sem("dist_done")
        gains_t, gains_ready = sem("gains_t"), sem("gains_ready")
        gu_norm = sem("gu_norm")
        gu_silu, gu_prod, gu_hi, gu_lo = sem("gu_silu"), sem("gu_prod"), sem("gu_hi"), sem("gu_lo")
        resid, xs_hi, xs_lo = sem("resid"), sem("xs_hi"), sem("xs_lo")
        sq_ready, sq_added = sem("sq_ready"), sem("sq_added")
        col_done, row_done = sem("col_done"), sem("row_done")
        nstep, rcol_ready, rdiag_ready, rstd_ready = sem("nstep"), sem("rcol_ready"), sem("rdiag_ready"), sem("rstd_ready")
        qk_ready, v_ready = sem("qk_ready"), sem("v_ready")
        f_biased = sem("f_biased")
        wf_hi, wf_lo, fl_done, f_step, f_act = sem("wf_hi"), sem("wf_lo"), sem("fl_done"), sem("f_step"), sem("f_act")
        half_resid = sem("half_resid")
        fcum_done, fk_done, bias_ready = sem("fcum_done"), sem("fk_done"), sem("bias_ready")
        chunk_bias = sem("chunk_bias")
        swa_bias = sem("swa_bias")
        k_swapped = sem("k_swapped")
        scores_done, logits_ready = sem("scores_done"), sem("logits_ready")
        exp_done, pt_done, pt_ready = sem("exp_done"), sem("pt_done"), sem("pt_ready")
        sb_abs, sb_e, sb_log, sb_sp, incl_done, sb_a = sem("sb_abs"), sem("sb_e"), sem("sb_log"), sem("sb_sp"), sem("incl_done"), sem("sb_a")
        norm_step, probs_ready, pv_done = sem("norm_step"), sem("probs_ready"), sem("pv_done")
        os_hi, os_lo = sem("os_hi"), sem("os_lo")
        p_t, p_hi, p_lo = sem("p_t"), sem("p_hi"), sem("p_lo")
        proj_ready, g_norm, g_sig, g_prod = sem("proj_ready"), sem("g_norm"), sem("g_sig"), sem("g_prod")
        y_ready, y_turned, y_low, y_high, stored = sem("y_ready"), sem("y_turned"), sem("y_low"), sem("y_high"), sem("stored")

        N_CONSTS, N_IDENT = 21, 2
        GU_START = 2

        def gu_bank(f):
            return 4 * (f // 2 % 2) + f % 2

        def gain(norm, m):
            col = (norm % 4) * DEPTH * KD + (norm // 4) * KD + m if norm < 4 * DEPTH else 4 * DEPTH * KD + m
            return gains[:, col:col + 1]

        def stream(norm):
            return xsB if norm == 4 else xsA

        heads = [(layer, group, h) for layer in range(DEPTH) for group in range(2) for h in range(HEADS)]
        is_sb = [layer == 0 and group == 1 for layer, group, h in heads]
        soft_no = [sum(not s for s in is_sb[:g]) for g in range(len(heads))]
        stick_no = [sum(is_sb[:g]) for g in range(len(heads))]

        def head_q(g):
            _, group, h = heads[g]
            r = HD * (h % 2)
            return slice(r, r + HD), 4 * group + h // 2

        def head_k(g):
            layer, group, h = heads[g]
            if layer == 1 and group == 1:
                return 4 if h // 4 == h % 2 else 5
            return 4 * group + h // 2

        def head_v(g):
            layer, group, h = heads[g]
            return GROUP_W * group + HD * (h // 4 if layer == 1 and group == 1 else h)

        IN_TILES = [in_tiles(layer) for layer in range(DEPTH)]
        FIRST_SLOT = (12, 8)
        SLOTS = 2 * HEADS + 3

        PLE_UNITS = {"p": (0, 1, 0, 1, 0, 1, 0, 0), "g": (1, 1, 1, 1, 1, 1, 1, 0)}

        def in_units(ph, n):
            tiles = IN_TILES[ph.layer]
            ends = n + 1 == len(tiles) or tiles[n + 1][0] > tiles[n][0]
            return 2 * (ph.c0 + tiles[n][0] + RING) + ends

        def in_bank(n):
            return n % 4 if n < 8 else (n - 8) % 3

        def slots(layer, n):
            return (n - FIRST_SLOT[layer],) if n >= FIRST_SLOT[layer] else ()

        def out_slots(layer, m):
            i = len(IN_TILES[layer]) - FIRST_SLOT[layer] + m
            return (i,) if i < SLOTS else ()

        def out_bank(layer, u):
            return (len(IN_TILES[layer]) - 8 + u) % 3

        def is_v(what):
            return what[0] == "v"

        def written(layer, n):
            tiles = [t for i in range(layer) for t in IN_TILES[i]] + IN_TILES[layer][:n + 1]
            v = is_v(tiles[-1][2])
            return (v_ready if v else qk_ready), sum(is_v(t[2]) == v for t in tiles)

        def last_written(layer, want):
            return written(layer, max(n for n, t in enumerate(IN_TILES[layer]) if want(t[2], t[3])))

        def weight_source(ph, r):
            i = ph.layer
            if ph.kind == "gu":
                w = (w_ffn1_gu, w_ffn2_gu)[ph.which]
                pair, up = r
                return w[i].rearrange("(k p) n -> p k n", p=P)[:, :, bass.ds(pair * 256 + up * D_FF, 256)]
            if ph.kind == "down":
                w = (w_ffn1_down, w_ffn2_down)[ph.which]
                m, half = r
                return w[i].rearrange("(k p) n -> p k n", p=P)[:, half * (KF // 2):(half + 1) * (KF // 2), bass.ds(m * P, P)]
            if ph.kind == "in":
                w = (w_in_even, w_in_odd)[i]
                if i == 1 and r >= 6:
                    r = (8, 6, 7)[r - 6]
                col = r * 256 + (HEADS if i == 0 and r >= 6 else 0)
                return w[0].rearrange("(k p) n -> p k n", p=P)[:, :, col:col + 256]
            if ph.kind == "out":
                w = (w_out_even, w_out_odd)[i]
                return w[0].rearrange("(k p) n -> p k n", p=P)[:, :, r * 256:(r + 1) * 256]
            if ph.kind == "gate":
                return w_ple_gate[i].rearrange("(k p) n -> p k n", p=P)[:, :, r * 256:(r + 1) * 256]
            return w_ple_proj[i].rearrange("(k p) n -> p k n", p=P)

        block = ctx.enter_context(nc.Block())

        @block.sync
        def _(sp):
            def load(ph, r, c, lap=0):
                if not (isinstance(lap, int) and c < RING):
                    sp.wait_ge(lo, 2 * (c - RING) + 2 + 2 * RING * lap)
                k, n = (KF // 2, P) if ph.kind == "down" else (KPLE, D_MODEL) if ph.kind == "proj" else (KD, 256)
                dst = raw[:, c % RING, 0:k * n].rearrange("p (k n) -> p k n", k=k)
                sp.dma_start(dst, weight_source(ph, r)).then_inc(landed[c % RING], 16)

            x_rows = x[0].rearrange("(t p) d -> p t d", p=P)
            for t in range(TOK):
                sp.dma_start(xin[:, t, :], x_rows[:, t, :]).then_inc(in_x, 16)
            for n, g in enumerate((ln_ffn1, ln_mix, ln_ffn2, ln_ple)):
                rows = DEPTH * KD
                sp.dma_start(gin[n * rows:(n + 1) * rows, :], g.rearrange("l (k p) -> (l k) p", p=P)).then_inc(in_g, 16)
            sp.dma_start(gin[4 * DEPTH * KD:(4 * DEPTH + 1) * KD, :], ln_final.rearrange("(k p) -> k p", p=P)).then_inc(in_g, 16)
            for ph in phases:
                c0 = ph.c0
                if ph.kind == "gu":
                    for r in range(RING):
                        load(ph, (r // 2, r % 2), c0 + r)
                    with sp.Fori(0, (ph.chunks - RING - 2) // RING) as i:
                        for r in range(RING):
                            load(ph, (2 * i + (r + RING) // 2, r % 2), c0 + RING + r, lap=i)
                    for r in range(ph.chunks - 2, ph.chunks):
                        load(ph, (r // 2, r % 2), c0 + r)
                elif ph.kind == "down":
                    with sp.Fori(0, ph.chunks // RING) as i:
                        for r in range(RING):
                            load(ph, (2 * i + r // 2, r % 2), c0 + r, lap=i)
                else:
                    for r in range(ph.chunks):
                        load(ph, r, c0 + r)
            out_rows = out[0].rearrange("(t p) d -> p t d", p=P)
            for half, written in enumerate((y_low, y_high)):
                for t in range(TOK):
                    sp.wait_ge(written, t + 1)
                    sl = slice(512 * half, 512 * (half + 1))
                    sp.dma_start(out_rows[:, t, sl], yN[:, t, sl]).then_inc(stored, 16)
            sp.wait_ge(stored, 2 * 16 * TOK)

        @block.gpsimd
        def _(pool):
            made = [0]

            def const(ins):
                made[0] += 1
                ins.then_inc(consts, 1)

            def settle():
                pool.wait_ge(consts, made[0])

            const(pool.memset(ident[:], 0.0))
            settle()
            diag = dict(compare_op=ALU.not_equal, base=0, pattern=[[-1, P]], channel_multiplier=1)
            const(pool.affine_select(out=ident[:], in_=ident[:], fill=1.0, **diag))
            const(pool.memset(identb[:], 0.0))
            const(pool.memset(cumtri[:], 1.0))
            const(pool.memset(negtri[:], -1.0))
            const(pool.memset(negones[:], -1.0))
            const(pool.memset(mask_sb[:], 0.0))
            const(pool.memset(mask_causal[:], 0.0))
            const(pool.memset(mask_chunk[:], 0.0))
            settle()
            const(pool.affine_select(out=identb[:], in_=identb[:], fill=1.0, **diag))
            const(pool.affine_select(out=cumtri[:, 0:P], in_=cumtri[:, 0:P], fill=0.0, compare_op=ALU.is_ge,
                                     base=0, pattern=[[1, P]], channel_multiplier=-1))
            const(pool.affine_select(out=negtri[:], in_=negtri[:], fill=0.0, compare_op=ALU.is_ge,
                                     base=0, pattern=[[-1, P]], channel_multiplier=1))
            const(pool.affine_select(out=mask_sb[:], in_=mask_sb[:], fill=-BIG, compare_op=ALU.is_gt,
                                     base=0, pattern=[[1, P]], channel_multiplier=-1))
            for col in (0, 2 * P):
                const(pool.affine_select(out=mask_causal[:, col:col + P], in_=mask_causal[:, col:col + P], fill=BIG,
                                         compare_op=ALU.is_ge, base=0, pattern=[[-1, P]], channel_multiplier=1))
            for col in (CHUNK, 2 * P + CHUNK):
                const(pool.memset(mask_chunk[0:CHUNK, col:col + CHUNK], BIG))
            const(pool.iota(dist_swa[:, 0:P], pattern=[[-1, P]], base=0, channel_multiplier=1,
                            allow_small_or_imprecise_dtypes=True))
            const(pool.iota(dist_swa[:, P:], pattern=[[-1, 2 * P]], base=P, channel_multiplier=1,
                            allow_small_or_imprecise_dtypes=True))
            const(pool.memset(rel_sb[:], 0.0))
            const(pool.memset(sqsum[:], 0.0))
            assert made[0] == N_CONSTS, made[0]

            def squares(norm):
                for m in range(KD):
                    R = KD * norm + m
                    pool.wait_ge(sq_ready, R + 1)
                    if m == 0:
                        if norm:
                            pool.wait_ge(col_done, norm)
                        pool.tensor_copy(sqsum[:], sq[:, R % 2]).then_inc(sq_added, 1)
                    else:
                        pool.wait_ge(sq_added, R)
                        pool.tensor_tensor(sqsum[:], sqsum[:], sq[:, R % 2], ALU.add).then_inc(sq_added, 1)

            settle()
            squares(0)
            pool.wait_ge(dist_abs, 1)
            pool.wait_ge(sq_added, KD)
            for rows, col, n in ((0, CHUNK, CHUNK), (0, P, CHUNK), (0, 2 * P + CHUNK, CHUNK), (CHUNK, P, P)):
                pool.memset(dist_swa[rows:rows + CHUNK, col:col + n], BIG * 100).then_inc(dist_done, 1)
            pool.wait_ge(dist_done, 4)
            for norm in range(1, 6):
                squares(norm)
            pool.wait_ge(rel_back, 16)
            pool.wait_ge(pv_done, 2 * HEADS)
            for n, (col, far) in enumerate(((0, P), (P, 2 * P), (2 * P, P))):
                pool.tensor_tensor(bias[:, :, col:col + P],
                                   mask_chunk[:, col:col + P].unsqueeze(1).broadcast_to([P, HEADS, P]),
                                   hankel[:, :, far:far - P:-1], ALU.subtract).then_inc(chunk_bias, 1)
            pool.wait_ge(dist_done, 4)
            for h in range(HEADS):
                g = 3 * HEADS + h
                if h >= 2:
                    pool.wait_ge(logits_ready, 2 * (soft_no[g - 2] + 1))
                pool.tensor_scalar(bias_swa[:, h % 2], dist_swa[:], 2.0 ** -(h + 1), None, ALU.mult).then_inc(swa_bias, 1)
            for norm in range(6, 9):
                squares(norm)

        @block.scalar
        def _(act):
            ptr = [0]

            def split_unit(u, ph, lap=0):
                c, half = u // 2, u % 2
                s, n = c % RING, ph.unit
                if half == 0:
                    act.wait_ge(landed[s], 16 * (c // RING + 1) + 16 * lap)
                    if c >= RING:
                        act.wait_ge(tile_done, tile_end[c - RING] + 2 * RING * lap)
                act.activation(wsp[:, s, 0, half * n:(half + 1) * n], raw[:, s, half * n:(half + 1) * n],
                               ACT.Copy).then_inc(hi, 1)

            def phase_of(u):
                return [ph for ph in phases if ph.c0 <= u // 2][-1]

            def advance(to):
                while ptr[0] < min(to, 2 * n_chunks):
                    split_unit(ptr[0], phase_of(ptr[0]))
                    ptr[0] += 1

            state = {"T": 0}

            def hidden_step(F, f, units):
                units[0]()
                act.wait_ge(gu_norm, F + 1 + GU_START)
                act.activation(silu[:], gate_n[:, 0], ACT.Silu).then_inc(gu_silu, 1)
                units[1]()
                act.wait_ge(gu_prod, F + 1)
                act.activation(hff[:, f, 0, :], hidden[:], ACT.Copy).then_inc(gu_hi, 1)

            def gate_up(ph):
                F0, c0 = ph.F0, ph.c0
                advance(2 * (c0 + RING))

                def straight(f):
                    def unit():
                        split_unit(ptr[0], phase_of(ptr[0]))
                        ptr[0] += 1
                    if F0 + f == 0:
                        act.wait_ge(rel_out, 16)
                    hidden_step(F0 + f, f, (unit, unit))

                for f in range(2):
                    straight(f)
                laps = (ph.chunks - 6) // RING
                with act.Fori(0, laps) as i:
                    for j in range(RING):
                        f = 2 + j
                        units = tuple((lambda q=ptr[0] + 2 * j + h: split_unit(q, ph, lap=i)) for h in range(2))
                        hidden_step(F0 + f + RING * i, RING * i + f, units)
                ptr[0] += 2 * RING * laps
                for f in range(2 + RING * laps, KF):
                    straight(f)
                state["T"] += 2 * KF

            def next_tile():
                state["T"] += 1
                act.wait_ge(tile_done, state["T"])

            def new_stream(norm, m):
                R = KD * norm + m
                act.wait_ge(resid, R + 1)
                if norm < 8:
                    act.activation(stream(norm)[:, m, 0, :], xT[:, m], ACT.Copy, scale=gain(norm, m)).then_inc(xs_hi, 1)
                if R >= 2:
                    act.wait_ge(sq_added, R - 1)
                act.activation(sq[:, R % 2], xT[:, m], ACT.Square).then_inc(sq_ready, 1)
                if norm == 8:
                    act.activation(yT[:, m], xT[:, m], ACT.Copy, scale=gain(norm, m)).then_inc(y_ready, 1)

            nc.scalar.preload_act_table_set("silu_and_others")
            act.dma_start(wf_raw[:], w_in_even[0].rearrange("(k p) n -> p k n", p=P)[:, :, 3 * GROUP_W:3 * GROUP_W + HEADS]).then_inc(in_small, 16)
            act.dma_start(bf[:], b_forget.broadcast_to([P, HEADS])).then_inc(in_small, 16)
            act.dma_start(nsink[:], sinks.broadcast_to([P, HEADS])).then_inc(in_small, 16)
            state["T"] += KD
            act.wait_ge(gains_ready, 1)
            for m in range(KD):
                new_stream(0, m)
                if m in (1, 4):
                    advance(ptr[0] + 1)
            advance(4)
            act.wait_ge(consts, N_CONSTS)
            act.dma_start(rel_sb[:, 0:2 * REL_CLIP + 1], rel_bias[0]).then_inc(in_rel, 16)
            act.wait_ge(in_small, 48)
            act.activation(wf[:, 0], wf_raw[:], ACT.Copy).then_inc(wf_hi, 1)
            act.wait_ge(rel_ext, 1)
            act.dma_start(rel_scratch.ap(), rel_sb[:]).then_inc(rel_out, 16)
            advance(2 * RING)

            def down(ph, norm):
                for m in range(KD):
                    state["T"] += 1
                    new_stream(norm, m)
                    if m < KD - 1:
                        advance(2 * (ph.c0 + 2 * m + 6))

            def mixer_in(ph, norm):
                if ph.layer == 1:
                    act.wait_ge(tile_done, state["T"])
                    src = bass.AP(rel_scratch, 0, [[1, P], [3 * P, HEADS], [1, 257]])
                    act.dma_start(hankel[:], src).then_inc(rel_back, 16)
                for n, (chunk, col, what, idx, scale) in enumerate(IN_TILES[ph.layer]):
                    next_tile()
                    if is_v(what):
                        if what == "v":
                            group, j, t = idx
                            start, w = GROUP_W * group + 256 * j, 256
                        else:
                            t, start, w = idx, GROUP_W, P
                        act.wait_ge(rcol_ready, norm + 1)
                        act.activation(vN[:, t, start:start + w], ps[:, in_bank(n), 0:w], ACT.Copy,
                                       scale=rcol[:, t:t + 1]).then_inc(v_ready, 1)
                    if not slots(ph.layer, n):
                        advance(in_units(ph, n))
                    if ph.layer == 1 and (what, idx) == ("vd", 0):
                        act.wait_ge(*written(1, n - 1))
                        act.dma_start(kT[0:HD, 5, :], kT[HD:P, 4, :]).then_inc(k_swapped, 16)
                        act.dma_start(kT[HD:P, 5, :], kT[0:HD, 4, :]).then_inc(k_swapped, 16)
                    if ph.layer == 0 and n == 0:
                        nc.scalar.preload_act_table_set("natural_log_exp_and_others")
                        act.wait_ge(f_step, 2)
                        act.activation(fa[:], fa[:], ACT.Exp, scale=-1.0).then_inc(f_act, 1)
                        act.wait_ge(f_act, 1)
                        act.activation(fa[:], fa[:], ACT.Ln, bias=1.0).then_inc(f_act, 1)
                    for i in slots(ph.layer, n):
                        attention_step(ph.layer, i)
                        advance(in_units(ph, n))

            def attention_step(layer, i):
                first, n = 2 * HEADS * layer, 2 * HEADS
                g = first + i
                if i < n:
                    s, b = g % 2, soft_no[g]
                    if not is_sb[g]:
                        for t in range(TOK):
                            act.wait_ge(logits_ready, 2 * b + t + 1)
                            sl = slice(0, P) if t == 0 else slice(P, LOGITS)
                            act.activation(probs[:, s, sl], probs[:, s, sl], ACT.Exp, bias=negmax[:, s, t:t + 1],
                                           scale=-1.0, accum_out=rowsum[:, g % 4, t:t + 1]).then_inc(exp_done, 1)
                        if g >= 3 * HEADS:
                            h = heads[g][2]
                            for t in range(TOK):
                                act.activation(sinkexp[:, g % 4, t:t + 1], nsink[:, h:h + 1], ACT.Exp,
                                               bias=negmax[:, s, t:t + 1], scale=-1.0).then_inc(exp_done, 1)
                    else:
                        k = stick_no[g]
                        act.wait_ge(sb_abs, k + 1)
                        act.activation(probs[:, s], probs[:, s], ACT.Exp, scale=-1.0).then_inc(sb_e, 1)
                        act.wait_ge(sb_e, k + 1)
                        act.activation(probs[:, s], probs[:, s], ACT.Ln, bias=1.0).then_inc(sb_log, 1)
                if 1 <= i <= n and not is_sb[g - 1]:
                    b = soft_no[g - 1]
                    act.wait_ge(pt_done, b + 1)
                    if g - 1 >= 2:
                        act.wait_ge(pv_done, g - 2)
                    act.activation(probsT[:, (g - 1) % 2], ps[:, BANK_PT, 0:LOGITS], ACT.Copy).then_inc(pt_ready, 1)
                if 1 <= i <= n and is_sb[g - 1]:
                    k = stick_no[g - 1]
                    act.wait_ge(incl_done, k + 1)
                    if g - 1 >= 2:
                        act.wait_ge(pv_done, g - 2)
                    act.activation(probsT[:, (g - 1) % 2], ps[:, BANK_S + (g - 1) % 2, 0:LOGITS], ACT.Exp).then_inc(sb_a, 1)
                if 3 <= i and (g - 3) % 2 == 1:
                    pair = (g - 3) // 2
                    act.wait_ge(pv_done, 2 * pair + 2)
                    act.activation(osp[:, pair % KD, 0, :], ps[:, BANK_O[pair % 2], 0:SEQ], ACT.Copy).then_inc(os_hi, 1)

            def mixer_out(ph, norm):
                for m in range(KD):
                    for i in out_slots(ph.layer, m):
                        attention_step(ph.layer, i)
                    next_tile()
                    advance(2 * (ph.c0 + RING))
                act.wait_ge(pv_done, 2 * HEADS * (ph.layer + 1))
                act.dma_start(pin[:], p[ph.layer, 0].rearrange("(t p) d -> p t d", p=P)).then_inc(in_p, 16)
                for m in range(KD):
                    next_tile()
                    new_stream(norm, m)
                    advance(2 * (ph.c0 + RING) + (m + 1) // 2)
                act.wait_ge(p_t, ph.layer + 1)
                act.activation(psp[:, :, 0, :], ps[:, 5, :].rearrange("p (k t) -> p k t", k=KPLE), ACT.Copy).then_inc(p_hi, 1)

            def ple(ph_proj, norm):
                layer = ph_proj.layer
                advance(2 * (ph_proj.c0 + 2))
                nc.scalar.preload_act_table_set("sigmoid_and_others")
                for kind, m in PLE_TILES:
                    next_tile()
                    if kind == "p":
                        act.activation(proj[:, m], ps[:, ple_bank(kind, m), 0:SEQ], ACT.Copy).then_inc(proj_ready, 1)
                    else:
                        act.wait_ge(g_norm, KD * layer + m + 1)
                        act.activation(silu[:], tile_s[:], ACT.Sigmoid).then_inc(g_sig, 1)
                        if m:
                            new_stream(norm, m - 1)
                    advance(ptr[0] + PLE_UNITS[kind][m])
                new_stream(norm, KD - 1)

            norm = 1
            for n, ph in enumerate(phases):
                if ph.kind == "gu":
                    gate_up(ph)
                elif ph.kind == "down":
                    down(ph, norm)
                    norm += 1
                elif ph.kind == "in":
                    mixer_in(ph, norm - 1)
                elif ph.kind == "out":
                    mixer_out(ph, norm)
                    norm += 1
                elif ph.kind == "proj":
                    ple(ph, norm)
                    norm += 1
            act.wait_ge(rcol_ready, 9)
            for t in range(TOK):
                act.wait_ge(y_turned, TOK + t + 1)
                act.activation(yN[:, t, 512:1024], ps[:, t, :], ACT.Copy, scale=rcol[:, t:t + 1]).then_inc(y_high, 1)

        @block.vector
        def _(dve):
            ptr = [0]

            def split_unit(u, ph, lap=0):
                c, half = u // 2, u % 2
                s, n = c % RING, ph.unit
                sl = slice(half * n, (half + 1) * n)
                dve.wait_ge(hi, u + 1 + 2 * RING * lap)
                dve.tensor_tensor(wsp[:, s, 1, sl], raw[:, s, sl], wsp[:, s, 0, sl].bitcast(F32), ALU.subtract).then_inc(lo, 1)

            def phase_of(u):
                return [ph for ph in phases if ph.c0 <= u // 2][-1]

            def advance(to):
                while ptr[0] < min(to, 2 * n_chunks):
                    split_unit(ptr[0], phase_of(ptr[0]))
                    ptr[0] += 1

            state = {"T": 0, "n": 0, "o": 0}

            def hidden_step(F, T, b, f, units):
                dve.wait_ge(tile_done, T)
                dve.tensor_tensor(gate_n[:], ps[:, b:b + 3:2, 0:SEQ], rstd[:].unsqueeze(1).broadcast_to([P, 2, SEQ]),
                                  ALU.mult).then_inc(gu_norm, 1)
                units[0]()
                dve.wait_ge(gu_silu, F + 1)
                dve.wait_ge(gu_norm, F + 1 + GU_START)
                dve.tensor_tensor(hidden[:], silu[:], gate_n[:, 1], ALU.mult).then_inc(gu_prod, 1)
                units[1]()
                dve.wait_ge(gu_prod, F + 1)
                dve.wait_ge(gu_hi, F + 1)
                dve.tensor_tensor(hff[:, f, 1, :], hidden[:], hff[:, f, 0, :].bitcast(F32), ALU.subtract).then_inc(gu_lo, 1)

            def gate_up(ph):
                F0, T0 = ph.F0, state["T"]
                advance(2 * (ph.c0 + RING))

                def straight(f):
                    def unit():
                        split_unit(ptr[0], phase_of(ptr[0]))
                        ptr[0] += 1
                    hidden_step(F0 + f, T0 + 4 * (f // 2) + f % 2 + 3, gu_bank(f), f, (unit, unit))

                for f in range(2):
                    straight(f)
                laps = (ph.chunks - 6) // RING
                with dve.Fori(0, laps) as i:
                    for j in range(RING):
                        f = 2 + j
                        units = tuple((lambda q=ptr[0] + 2 * j + h: split_unit(q, ph, lap=i)) for h in range(2))
                        hidden_step(F0 + f + RING * i, T0 + 4 * (f // 2) + f % 2 + 3 + 2 * RING * i, gu_bank(f),
                                    RING * i + f, units)
                ptr[0] += 2 * RING * laps
                for f in range(2 + RING * laps, KF):
                    straight(f)
                state["T"] += 2 * KF

            def next_tile():
                state["T"] += 1
                dve.wait_ge(tile_done, state["T"])

            def low_part(norm, m):
                R = KD * norm + m
                if norm == 8:
                    return
                dve.wait_ge(xs_hi, R + 1)
                xs = stream(norm)
                dve.wait_ge(resid, R + 1)
                dve.scalar_tensor_tensor(xs[:, m, 1, :], xT[:, m], gain(norm, m), xs[:, m, 0, :].bitcast(F32),
                                         ALU.mult, ALU.subtract).then_inc(xs_lo, 1)

            def inverse_root(norm):
                def step(ins):
                    state["n"] += 1
                    ins.then_inc(nstep, 1)
                    dve.wait_ge(nstep, state["n"])
                dve.wait_ge(col_done, norm + 1)
                step(dve.tensor_scalar(var[:], ps[:, BANK_COL, 0:TOK], 1.0 / D_MODEL, EPS, ALU.mult, ALU.add))
                step(dve.tensor_scalar(rcol[:].bitcast(I32), var[:].bitcast(I32), 1, None, ALU.logical_shift_right))
                step(dve.tensor_scalar(rcol[:].bitcast(I32), rcol[:].bitcast(I32), -1.0, float(MAGIC), ALU.mult, ALU.add))
                step(dve.tensor_scalar(nhalf[:], var[:], -0.5, None, ALU.mult))
                for _ in range(2):
                    step(dve.tensor_tensor(rtmp[:], rcol[:], rcol[:], ALU.mult))
                    step(dve.tensor_tensor(rtmp[:], rtmp[:], nhalf[:], ALU.mult))
                    step(dve.scalar_tensor_tensor(rcol[:], rtmp[:], 1.5, rcol[:], ALU.add, ALU.mult))
                step(dve.tensor_tensor(rtmp[:], rcol[:], rcol[:], ALU.mult))
                step(dve.tensor_tensor(rtmp[:], rtmp[:], nhalf[:], ALU.mult))
                last = dve.scalar_tensor_tensor(rcol[:], rtmp[:], 1.5, rcol[:], ALU.add, ALU.mult)
                last.then_inc(rcol_ready, 1)
                dve.wait_ge(rcol_ready, norm + 1)
                if norm == 8:
                    return
                for t in range(TOK):
                    dve.tensor_scalar(rdiag[:, t], ident[:], rcol[:, t:t + 1], None, ALU.mult).then_inc(rdiag_ready, 1)
                dve.wait_ge(row_done, norm + 1)
                dve.tensor_scalar(rstd[:], ps[:, BANK_ROW, 0:SEQ], -1.0, None, ALU.mult).then_inc(rstd_ready, 1)
                dve.wait_ge(rstd_ready, norm + 1)

            dve.memset(rtmp[:], 0.0).then_inc(gu_norm, GU_START)
            dve.wait_ge(gains_t, 1)
            dve.tensor_copy(gains[:], ps[:, 6, 0:(4 * DEPTH + 1) * KD]).then_inc(gains_ready, 1)
            dve.wait_ge(gains_ready, 1)
            for m in range(KD):
                dve.wait_ge(tile_done, m + 1)
                dve.tensor_copy(xT[:, m], ps[:, m % 4, 0:SEQ]).then_inc(resid, 1)
                if m:
                    low_part(0, m - 1)
                if m in (2, 5):
                    advance(ptr[0] + 1)
            low_part(0, KD - 1)
            advance(4)
            state["T"] = KD
            dve.wait_ge(consts, N_CONSTS)
            dve.tensor_scalar(dist_swa[:].bitcast(I32), dist_swa[:].bitcast(I32), NO_SIGN, None, ALU.bitwise_and).then_inc(dist_abs, 1)
            dve.wait_ge(in_small, 48)
            dve.tensor_scalar(nsink[:], nsink[:], -1.0, None, ALU.mult).then_inc(f_step, 1)
            dve.wait_ge(wf_hi, 1)
            dve.tensor_tensor(wf[:, 1], wf_raw[:], wf[:, 0].bitcast(F32), ALU.subtract).then_inc(wf_lo, 1)
            dve.wait_ge(in_rel, 16)
            dve.tensor_copy(rel_sb[:, 257:], rel_sb[:, 256:257].broadcast_to([HEADS, 3 * P - 257])).then_inc(rel_ext, 1)

            def down(ph, norm):
                for m in range(KD):
                    next_tile()
                    dve.scalar_tensor_tensor(xT[:, m], ps[:, m % 2, 0:SEQ], 0.5, xT[:, m], ALU.mult, ALU.add).then_inc(resid, 1)
                    if m < KD - 1:
                        advance(ptr[0] + 1)
                    low_part(norm, m)
                    if m < KD - 1:
                        advance(2 * (ph.c0 + 2 * m + 6))

            def forget_gate():
                fp = ps[:, BANK_F, 0:TOK * 2 * HEADS].rearrange("p (t s h) -> p t s h", t=TOK, s=2)
                dve.wait_ge(fl_done, 1)
                for t in range(TOK):
                    last = dve.scalar_tensor_tensor(fl[:, t], fp[:, t, 0], rcol[:, t:t + 1], bf[:], ALU.mult, ALU.add)
                last.then_inc(f_biased, 1)
                dve.wait_ge(f_biased, 1)
                for t in range(TOK):
                    last = dve.scalar_tensor_tensor(fl[:, t], fp[:, t, 1], rcol[:, t:t + 1], fl[:, t], ALU.mult, ALU.add)
                last.then_inc(f_biased, 1)
                dve.wait_ge(f_biased, 2)
                dve.tensor_scalar(fa[:].bitcast(I32), fl[:].bitcast(I32), NO_SIGN, None, ALU.bitwise_and).then_inc(f_step, 1)
                dve.wait_ge(f_act, 2)
                dve.scalar_tensor_tensor(logf[:], fl[:], 0.0, fa[:], ALU.min, ALU.subtract).then_inc(f_step, 1)

            def mixer_in(ph, norm):
                for n, (chunk, col, what, idx, scale) in enumerate(IN_TILES[ph.layer]):
                    if n == 0:
                        inverse_root(norm)
                    bank = in_bank(n)
                    next_tile()
                    if not is_v(what):
                        dst = (qT if what == "q" else kT)[:, idx, :]
                        dve.scalar_tensor_tensor(dst, ps[:, bank, 0:SEQ], scale, rstd[:], ALU.mult, ALU.mult).then_inc(qk_ready, 1)
                    if not slots(ph.layer, n):
                        advance(in_units(ph, n))
                    if ph.layer == 0 and n == 0:
                        forget_gate()
                    if ph.layer == 0 and n == 3:
                        dve.wait_ge(fcum_done, 1)
                        dve.tensor_copy(fcum[:], ps[:, BANK_F, 0:TOK * HEADS].rearrange("p (t h) -> p t h", t=TOK)).then_inc(f_step, 1)
                        dve.wait_ge(f_step, 4)
                    if ph.layer == 0 and 4 <= n < 4 + HEADS:
                        h = n - 4
                        dve.wait_ge(fk_done, h + 1)
                        fk = ps[:, BANK_S + h % 2, 0:SEQ]
                        dve.scalar_tensor_tensor(bias[:, h, 0:P], fk[:, 0:P], fcum[:, 0, h:h + 1], mask_causal[:, 0:P],
                                                 ALU.subtract, ALU.add)
                        dve.scalar_tensor_tensor(bias[:, h, P:], fk, fcum[:, 1, h:h + 1], mask_causal[:, P:],
                                                 ALU.subtract, ALU.add).then_inc(bias_ready, 1)
                    for i in slots(ph.layer, n):
                        attention_step(ph.layer, i, in_units(ph, n - 1))

            def attention_step(layer, i, units):
                first, n = 2 * HEADS * layer, 2 * HEADS
                if layer == 1 and i == 0:
                    dve.wait_ge(chunk_bias, 3)
                g = first + i
                s = g % 2
                if i < n:
                    _, group, h = heads[g]
                    dve.wait_ge(scores_done, g + 1)
                    S = ps[:, BANK_S + s, 0:LOGITS]
                    if g >= 2:
                        if is_sb[g - 2]:
                            dve.wait_ge(incl_done, stick_no[g - 2] + 1)
                        else:
                            dve.wait_ge(pt_done, soft_no[g - 2] + 1)
                    if not is_sb[g]:
                        if layer == 0:
                            dve.wait_ge(bias_ready, h + 1)
                        if g >= 3 * HEADS:
                            dve.wait_ge(swa_bias, h + 1)
                        B = bias_swa[:, h % 2] if g >= 3 * HEADS else bias[:, h]
                        start = nsink[:, h:h + 1] if g >= 3 * HEADS else 3e38
                        for t in range(TOK):
                            sl = slice(0, P) if t == 0 else slice(P, LOGITS)
                            dve.tensor_tensor_reduce(probs[:, s, sl], S[:, sl], B[:, sl], 1.0, start, ALU.add, ALU.min,
                                                     negmax[:, s, t:t + 1]).then_inc(logits_ready, 1)
                    else:
                        dve.tensor_scalar(probs[:, s].bitcast(I32), S.bitcast(I32), NO_SIGN, None, ALU.bitwise_and).then_inc(sb_abs, 1)
                advance(units)
                if i < n and not is_sb[g]:
                    def step(ins):
                        state["o"] += 1
                        ins.then_inc(norm_step, 1)
                        dve.wait_ge(norm_step, state["o"])
                    slot = g % 4
                    if g >= 3 * HEADS:
                        dve.wait_ge(exp_done, 2 * soft_no[3 * HEADS] + 4 * (g - 3 * HEADS + 1))
                        step(dve.tensor_tensor(rowsum[:, slot], rowsum[:, slot], sinkexp[:, slot], ALU.add))
                    else:
                        dve.wait_ge(exp_done, 2 * (soft_no[g] + 1))
                    step(dve.reciprocal(rinv[:, slot], rowsum[:, slot]))
                    for t, sl in ((0, slice(0, P)), (1, slice(P, LOGITS))):
                        last = dve.tensor_scalar(probs[:, g % 2, sl], probs[:, g % 2, sl], rinv[:, slot, t:t + 1], None, ALU.mult)
                    last.then_inc(probs_ready, 1)
                if i < n and is_sb[g]:
                    dve.wait_ge(sb_log, stick_no[g] + 1)
                    dve.scalar_tensor_tensor(probs[:, s], S, 0.0, probs[:, s], ALU.max, ALU.add).then_inc(sb_sp, 1)
                if 3 <= i and (g - 3) % 2 == 1:
                    pair = (g - 3) // 2
                    dve.wait_ge(os_hi, pair + 1)
                    dve.tensor_tensor(osp[:, pair % KD, 1, :], ps[:, BANK_O[pair % 2], 0:SEQ], osp[:, pair % KD, 0, :].bitcast(F32),
                                      ALU.subtract).then_inc(os_lo, 1)

            def mixer_out(ph, norm):
                for m in range(KD):
                    for i in out_slots(ph.layer, m):
                        attention_step(ph.layer, i, 2 * (ph.c0 + RING) - (m == 0))
                    next_tile()
                    dve.tensor_tensor(xT[:, m], ps[:, out_bank(ph.layer, m), 0:SEQ], xT[:, m], ALU.add).then_inc(half_resid, 1)
                    advance(2 * (ph.c0 + RING))
                for m in range(KD):
                    next_tile()
                    dve.wait_ge(half_resid, KD * ph.layer + m + 1)
                    dve.tensor_tensor(xT[:, m], ps[:, out_bank(ph.layer, KD + m), 0:SEQ], xT[:, m], ALU.add).then_inc(resid, 1)
                    if m:
                        low_part(norm, m - 1)
                    advance(2 * (ph.c0 + RING) + m // 2)
                low_part(norm, KD - 1)
                advance(2 * (ph.c0 + RING + 2))
                dve.wait_ge(p_hi, ph.layer + 1)
                dve.tensor_tensor(psp[:, :, 1, :], ps[:, 5, :].rearrange("p (k t) -> p k t", k=KPLE),
                                  psp[:, :, 0, :].bitcast(F32), ALU.subtract).then_inc(p_lo, 1)

            def ple(ph_proj, norm):
                layer = ph_proj.layer
                advance(2 * (ph_proj.c0 + 2))
                due = 0
                for kind, m in PLE_TILES:
                    if (kind, m) == ("p", 5):
                        inverse_root(norm - 1)
                    next_tile()
                    if kind == "g":
                        dve.tensor_tensor(tile_s[:], ps[:, ple_bank(kind, m), 0:SEQ], rstd[:], ALU.mult).then_inc(g_norm, 1)
                    if (kind, m) != ("g", KD - 1):
                        advance(ptr[0] + due)
                        due = PLE_UNITS[kind][m]
                    if kind == "g":
                        dve.wait_ge(proj_ready, KD * layer + m + 1)
                        dve.wait_ge(g_sig, KD * layer + m + 1)
                        dve.tensor_tensor(silu[:], silu[:], proj[:, m], ALU.mult).then_inc(g_prod, 1)
                        dve.wait_ge(g_prod, KD * layer + m + 1)
                        dve.tensor_tensor(xT[:, m], xT[:, m], silu[:], ALU.add).then_inc(resid, 1)
                        if m:
                            low_part(norm, m - 1)
                low_part(norm, KD - 1)
                advance(ptr[0] + due)

            norm = 1
            for n, ph in enumerate(phases):
                if ph.kind == "gu":
                    inverse_root(norm - 1)
                    gate_up(ph)
                elif ph.kind == "down":
                    down(ph, norm)
                    norm += 1
                elif ph.kind == "in":
                    mixer_in(ph, norm - 1)
                elif ph.kind == "out":
                    mixer_out(ph, norm)
                    norm += 1
                elif ph.kind == "proj":
                    ple(ph, norm)
                    norm += 1
            inverse_root(8)
            for t in range(TOK):
                dve.wait_ge(y_turned, t + 1)
                dve.tensor_scalar(yN[:, t, 0:512], ps[:, 4 + t, :], rcol[:, t:t + 1], None, ALU.mult).then_inc(y_low, 1)

        @block.tensor
        def _(pe):
            reader = {}

            def reuse(bank):
                if bank in reader:
                    pe.wait_ge(*reader[bank])

            def product(bank, weights, moving, first, last, ready=None):
                whi, wlo = weights
                if ready is not None:
                    pe.wait_ge(*ready)
                out_ = ps[:, bank, 0:SEQ]
                pe.matmul(out_, whi, moving[:, 0, :], start=first, stop=False)
                pe.matmul(out_, whi, moving[:, 1, :], start=False, stop=False)
                return pe.matmul(out_, wlo, moving[:, 0, :], start=False, stop=last)

            def chunk_w(slot, k, col, width=256):
                base = k * width + col
                return wsp[:, slot, 0, base:base + P], wsp[:, slot, 1, base:base + P]

            def tile8(bank, slot, col, xs, xs_base=None, sem_=None):
                for k in range(KD):
                    ready = (sem_, xs_base + k + 1) if xs_base is not None else None
                    mm = product(bank, chunk_w(slot, k, col), xs[:, k], k == 0, k == KD - 1, ready)
                mm.then_inc(tile_done, 1)
                return mm

            def column_sums(norm):
                pe.wait_ge(sq_added, KD * (norm + 1))
                if norm in (2, 6):
                    pe.wait_ge(os_lo, KD * (1 + norm // 6))
                for t in range(TOK):
                    mm = pe.matmul(ps[:, BANK_COL, t:t + 1], sqsum[:, t * P:(t + 1) * P], cumtri[:, 2 * P - 1:2 * P],
                                   start=True, stop=True)
                mm.then_inc(col_done, 1)

            def spread_rows(norm):
                if norm == 2 or norm == 6:
                    pe.wait_ge(pt_ready, soft_no[-1] + 1 if norm == 6 else HEADS)
                for t in range(TOK):
                    pe.wait_ge(rdiag_ready, 2 * norm + t + 1)
                    mm = pe.matmul(ps[:, BANK_ROW, t * P:(t + 1) * P], negones[:], rdiag[:, t], start=True, stop=True)
                mm.then_inc(row_done, 1)

            def chunk_ready(c, lap=0):
                pe.wait_ge(lo, 2 * c + 2 + 2 * RING * lap)

            def gate_up(ph, norm):
                c0, F0 = ph.c0, ph.F0
                xs = stream(norm)
                for r in range(2):
                    chunk_ready(c0 + r)
                    for n in range(2):
                        bank = 2 * r + n
                        reuse(bank)
                        tile8(bank, (c0 + r) % RING, n * P, xs, KD * norm if (r, n) == (0, 0) else None, xs_lo)
                        if (r, n) == (0, 0):
                            column_sums(norm)
                        if (r, n) == (1, 0):
                            spread_rows(norm)
                pe.wait_ge(rstd_ready, norm + 1)
                if ph.which == 1:
                    pe.wait_ge(p_lo, ph.layer + 1)
                with pe.Fori(0, (ph.chunks - 2) // RING) as i:
                    for r in range(RING):
                        c, pair = c0 + 2 + r, 1 + r // 2
                        chunk_ready(c, lap=i)
                        for n in range(2):
                            if r % 2 == 0:
                                pe.wait_ge(gu_norm, F0 + 2 * (pair - 2) + n + 1 + GU_START + RING * i)
                            tile8(gu_bank(2 * pair) + 2 * (r % 2) + n, c % RING, n * P, xs)
                for b in range(4):
                    reader[b] = (gu_norm, F0 + KF - 1 + b % 2 + GU_START)

            def down(ph, norm):
                half = KF // 2
                R0 = KD * (norm + 1)

                def row_tile(m, lap=0):
                    bank = m % 2
                    for part in range(2):
                        c = ph.c0 + 2 * m + part
                        chunk_ready(c, lap)
                        for k in range(half):
                            f = part * half + k
                            ready = (gu_lo, ph.F0 + f + 1) if m == 0 else None
                            mm = product(bank, chunk_w(c % RING, k, 0, P), hff[:, f], f == 0, f == KF - 1, ready)
                    mm.then_inc(tile_done, 1)

                for m in range(2):
                    reuse(m)
                    row_tile(m)
                with pe.Fori(0, KD // 2 - 1) as i:
                    for m in (2, 3):
                        pe.wait_ge(resid, R0 + m - 1 + 2 * i)
                        row_tile(m, lap=i)
                for b in range(2):
                    reader[b] = (resid, R0 + KD - 1 + b)

            def token_tile(out_, t, xs, weights):
                for k in range(KD):
                    w = weights(k)
                    xhi, xlo = xs[:, k, 0, t * P:(t + 1) * P], xs[:, k, 1, t * P:(t + 1) * P]
                    pe.matmul(out_, xhi, w[:, 0], start=k == 0, stop=False)
                    pe.matmul(out_, xhi, w[:, 1], start=False, stop=False)
                    mm = pe.matmul(out_, xlo, w[:, 0], start=False, stop=k == KD - 1)
                return mm

            def forget_logits(xs):
                pe.wait_ge(wf_lo, 1)
                for t in range(TOK):
                    out_ = ps[:, BANK_F, 2 * HEADS * t:2 * HEADS * (t + 1)]
                    for k in range(KD):
                        mm = pe.matmul(out_, xs[:, k, 0, t * P:(t + 1) * P], wf[:, :, k, :], start=k == 0, stop=True,
                                       skip_group_check=k > 0)
                        mm = pe.matmul(out_[:, 0:HEADS], xs[:, k, 1, t * P:(t + 1) * P], wf[:, 0, k, :], start=False,
                                       stop=True, skip_group_check=True)
                mm.then_inc(fl_done, 1)

            def forget_sums():
                tri, ones = cumtri[:, 0:P], cumtri[:, P:]
                pe.wait_ge(f_step, 3)
                pe.matmul(ps[:, BANK_F, 0:HEADS], tri, logf[:, 0], start=True, stop=True)
                pe.matmul(ps[:, BANK_F, HEADS:2 * HEADS], ones, logf[:, 0], start=True, stop=False)
                pe.matmul(ps[:, BANK_F, HEADS:2 * HEADS], tri, logf[:, 1], start=False, stop=True).then_inc(fcum_done, 1)

            def forget_keys(h):
                bank = BANK_S + h % 2
                if h >= 2:
                    pe.wait_ge(bias_ready, h - 1)
                pe.matmul(ps[:, bank, P:SEQ], logf[:, 1, h:h + 1].broadcast_to([P, P]), cumtri[:, 0:P], start=True, stop=True)
                pe.matmul(ps[:, bank, 0:SEQ], logf[:, 0, h:h + 1].broadcast_to([P, P]), cumtri[:], start=False, stop=True,
                          skip_group_check=True).then_inc(fk_done, 1)

            def mixer_in(ph, norm):
                xs = stream(norm)
                for n, (chunk, col, what, idx, scale) in enumerate(IN_TILES[ph.layer]):
                    bank, c = in_bank(n), ph.c0 + chunk
                    chunk_ready(c)
                    reuse(bank)
                    if what in "qk":
                        tile8(bank, c % RING, col, xs, KD * norm if n == 0 else None, xs_lo)
                    else:
                        t, w = (idx[2], 256) if what == "v" else (idx, P)
                        view = wsp[:, c % RING, :, 0:KD * 256].rearrange("p s (k n) -> p s k n", k=KD)
                        token_tile(ps[:, bank, 0:w], t, xs, lambda k: view[:, :, k, col:col + w]).then_inc(tile_done, 1)
                    reader[bank] = written(ph.layer, n)
                    if n == 0:
                        column_sums(norm)
                    if n == 2:
                        spread_rows(norm)
                        if ph.layer == 0:
                            forget_logits(xs)
                    if ph.layer == 0 and n == 3:
                        forget_sums()
                    if ph.layer == 0 and 4 <= n < 4 + HEADS:
                        forget_keys(n - 4)
                    for i in slots(ph.layer, n):
                        attention_step(ph.layer, i, norm)

            def scores(g):
                layer, group, h = heads[g]
                s, (rows, qt), kt = g % 2, head_q(g), head_k(g)
                S = ps[:, BANK_S + s]
                held = 4 if layer == 1 and group == 1 else kt
                pe.wait_ge(*last_written(layer, lambda what, idx: (what, idx) in (("q", qt), ("k", held))))
                if layer == 1 and group == 1 and kt == 5:
                    pe.wait_ge(k_swapped, 32)
                if g >= 2:
                    if is_sb[g - 2]:
                        pe.wait_ge(sb_a, stick_no[g - 2] + 1)
                    else:
                        pe.wait_ge(logits_ready, 2 * (soft_no[g - 2] + 1))
                if not is_sb[g]:
                    for t, sl, keys in ((0, slice(0, P), P), (1, slice(P, LOGITS), SEQ)):
                        mm = pe.matmul(S[:, sl], qT[rows, qt, t * P:(t + 1) * P], kT[rows, kt, 0:keys], start=True, stop=True)
                else:
                    pe.matmul(S[:, 0:P], identb[:], mask_sb[:], start=True, stop=True)
                    pe.matmul(S[:, 2 * P:LOGITS], identb[:], mask_sb[:], start=False, stop=True, skip_group_check=True)
                    pe.matmul(S[:, 0:SEQ], kT[rows, kt, 0:P], qT[rows, qt, :], start=False, stop=True, skip_group_check=True)
                    mm = pe.matmul(S[:, 2 * P:LOGITS], kT[rows, kt, P:SEQ], qT[rows, qt, P:SEQ], start=False, stop=True,
                                   skip_group_check=True)
                mm.then_inc(scores_done, 1)

            def middle(g):
                s = g % 2
                if not is_sb[g]:
                    pe.wait_ge(probs_ready, soft_no[g] + 1)
                    if soft_no[g]:
                        pe.wait_ge(pt_ready, soft_no[g])
                    for b in range(3):
                        mm = pe.transpose(ps[:, BANK_PT, b * P:(b + 1) * P], probs[:, s, b * P:(b + 1) * P], ident[:])
                    mm.then_inc(pt_done, 1)
                else:
                    S, sp_ = ps[:, BANK_S + s], probs[:, s]
                    pe.wait_ge(sb_sp, stick_no[g] + 1)
                    pe.matmul(S[:, 0:SEQ], negtri[:], sp_[:, 0:SEQ], start=False, stop=True, skip_group_check=True)
                    pe.matmul(S[:, P:SEQ], negones[:], sp_[:, SEQ:LOGITS], start=False, stop=True, skip_group_check=True)
                    pe.matmul(S[:, SEQ:LOGITS], negtri[:], sp_[:, SEQ:LOGITS], start=False, stop=True,
                              skip_group_check=True).then_inc(incl_done, 1)

            def values(g):
                s, v = g % 2, head_v(g)
                layer, group, h = heads[g]
                if layer == 1 and group == 1:
                    pe.wait_ge(*last_written(layer, lambda what, idx: what == "vd"))
                else:
                    pe.wait_ge(*last_written(layer, lambda what, idx: what == "v" and idx[:2] == (group, h // 4)))
                if is_sb[g]:
                    pe.wait_ge(sb_a, stick_no[g] + 1)
                else:
                    pe.wait_ge(pt_ready, soft_no[g] + 1)
                pair, rows = g // 2, slice(HD * (g % 2), HD * (g % 2 + 1))
                if pair % KD < 2:
                    reuse(BANK_O[pair % 2])
                else:
                    pe.wait_ge(os_lo, pair - 1)
                V = vN[:, :, v:v + HD]
                O = ps[rows, BANK_O[pair % 2], :]
                pe.matmul(O[:, 0:SEQ], V[:, 0], probsT[:, s, 0:SEQ], start=True, stop=False)
                pe.matmul(O[:, P:SEQ], V[:, 1], probsT[:, s, SEQ:LOGITS], start=False, stop=True).then_inc(pv_done, 1)

            def attention_step(layer, i, norm, tile=None):
                first, n = 2 * HEADS * layer, 2 * HEADS
                g = first + i
                if i == 0:
                    pe.wait_ge(rstd_ready, norm + 1)
                    if layer == 0:
                        pe.wait_ge(bias_ready, HEADS)
                        pe.wait_ge(f_step, 4)
                    else:
                        pe.wait_ge(p_lo, 1)
                if i < n:
                    scores(g)
                if tile is not None:
                    tile()
                if 1 <= i <= n:
                    middle(g - 1)
                if 2 <= i <= n + 1:
                    values(g - 2)
                if i == n + 2:
                    for b in range(2):
                        reader[BANK_O[b]] = (os_lo, (first + n) // 2 - 1 + b)

            def out_half(ph, m, half, norm):
                bank, c = out_bank(ph.layer, KD * half + m), ph.c0 + m // 2
                chunk_ready(c)
                reuse(bank)
                for k in range(KD // 2):
                    f = KD // 2 * half + k
                    ready = (os_lo, KD * ph.layer + f + 1) if m == 0 else None
                    mm = product(bank, chunk_w(c % RING, f, (m % 2) * P), osp[:, f], k == 0, k == KD // 2 - 1, ready)
                mm.then_inc(tile_done, 1)
                reader[bank] = (half_resid, KD * ph.layer + m + 1) if half == 0 else (resid, KD * (norm + 1) + m + 1)

            def mixer_out(ph, norm):
                for m in range(KD):
                    if out_slots(ph.layer, m):
                        attention_step(ph.layer, out_slots(ph.layer, m)[0], norm, lambda: out_half(ph, m, 0, norm))
                    else:
                        out_half(ph, m, 0, norm)
                for m in range(KD):
                    out_half(ph, m, 1, norm)
                    if m == 5:
                        pe.wait_ge(in_p, 16 * (ph.layer + 1))
                        for k in range(KPLE):
                            for t in range(TOK):
                                mm = pe.transpose(ps[:, 5, k * SEQ + t * P:k * SEQ + (t + 1) * P], pin[:, t, k * P:(k + 1) * P], ident[:])
                        mm.then_inc(p_t, 1)

            def ple(ph_proj, ph_gate, norm):
                for kind, m in PLE_TILES:
                    bank = ple_bank(kind, m)
                    c = ph_proj.c0 if kind == "p" else ph_gate.c0 + m // 2
                    chunk_ready(c)
                    reuse(bank)
                    if kind == "p":
                        if m == 0:
                            pe.wait_ge(p_lo, ph_proj.layer + 1)
                        for k in range(KPLE):
                            mm = product(bank, chunk_w(c % RING, k, m * P, D_MODEL), psp[:, k], k == 0, k == KPLE - 1)
                        mm.then_inc(tile_done, 1)
                    else:
                        tile8(bank, c % RING, (m % 2) * P, stream(norm), KD * norm if m == 0 else None, xs_lo)
                    reader[bank] = (proj_ready if kind == "p" else g_norm, KD * ph_proj.layer + m + 1)
                    if (kind, m) == ("p", 4):
                        column_sums(norm)
                    if (kind, m) == ("g", 0):
                        spread_rows(norm)

            pe.wait_ge(consts, N_IDENT)
            pe.wait_ge(in_g, 16 * 5)
            G = (4 * DEPTH + 1) * KD
            pe.transpose(ps[:, 6, 0:G], gin[0:G, :], ident[0:G, 0:G]).then_inc(gains_t, 1)
            pe.wait_ge(in_x, 16 * TOK)
            for m in range(KD):
                if m >= 4:
                    pe.wait_ge(resid, m - 3)
                for t in range(TOK):
                    mm = pe.transpose(ps[:, m % 4, t * P:(t + 1) * P], xin[:, t, m * P:(m + 1) * P], ident[:])
                mm.then_inc(tile_done, 1)
                reader[m % 4] = (resid, m + 1)
            pe.wait_ge(consts, N_CONSTS)
            norm = 0
            for n, ph in enumerate(phases):
                if ph.kind == "gu":
                    gate_up(ph, norm)
                elif ph.kind == "down":
                    down(ph, norm)
                    norm += 1
                elif ph.kind == "in":
                    mixer_in(ph, norm)
                elif ph.kind == "out":
                    mixer_out(ph, norm)
                    norm += 1
                elif ph.kind == "proj":
                    ple(ph, phases[n + 1], norm)
                    norm += 1
            def result(half):
                for t in range(TOK):
                    bank = (4, 0)[half] + t
                    reuse(bank)
                    for j in range(4):
                        m = 4 * half + j
                        pe.wait_ge(y_ready, m + 1)
                        mm = pe.transpose(ps[:, bank, j * P:(j + 1) * P], yT[:, m, t * P:(t + 1) * P], ident[:])
                    mm.then_inc(y_turned, 1)

            result(0)
            column_sums(8)
            result(1)


_INS = ['x', 'p', 'ln_ffn1', 'w_ffn1_gu', 'w_ffn1_down', 'ln_mix', 'w_in_even', 'b_forget', 'w_out_even', 'w_in_odd',
        'rel_bias', 'sinks', 'w_out_odd', 'ln_ffn2', 'w_ffn2_gu', 'w_ffn2_down', 'ln_ple', 'w_ple_gate', 'w_ple_proj',
        'ln_final']


def kernel(**inputs):
    import numpy as _np
    import concourse.bacc as _bacc
    from concourse import mybir as _mybir
    from concourse.bass_utils import run_bass_kernel_spmd as _run

    nc = _bacc.Bacc("TRN2", target_bir_lowering=False, num_devices=1)
    arrays, args = {}, []
    for name in _INS:
        a = _np.ascontiguousarray(inputs[name])
        arrays[f"in_{name}_dram"] = a
        args.append(nc.dram_tensor(f"in_{name}_dram", a.shape, _mybir.dt.from_np(a.dtype), kind="ExternalInput").ap())
    args.append(nc.dram_tensor("out_0_dram", (1, SEQ, D_MODEL), _mybir.dt.float32, kind="ExternalOutput").ap())
    trunk(nc, *args)
    r = _run(nc, [arrays], core_ids=[0])
    return r.results[0]["out_0_dram"]
```
